# Optimizing a Trainium2 kernel written in Bass

```python
import jax, jax.numpy as jnp
from jax import lax
import numpy as np

D_MODEL = 1024
BATCH = 1
SEQ = 2048
DEPTH = 1
DEC_BATCH = 8
DEC_SEQ = 4
PAST_LEN = 16384
PAGE_SIZE = 128

MIX_WIDTH = D_MODEL
N_MIXERS = 4
GROUP_WIDTH = MIX_WIDTH // N_MIXERS
N_SUB = 4
SUB_DIM = GROUP_WIDTH // N_SUB
POOL_WINDOWS = (2, 4, 8, 16)
POOL_BUF = max(POOL_WINDOWS) - 1
CONV_WIDTH = 31
SHORT_WIDTH = 3
CHUNK = 128
D_FF = 4 * D_MODEL
EPS = 1e-6
IN_WIDTH = GROUP_WIDTH * (1 + 2 + 2 + 3)

kernel_name = "hybrid_parallel_pool_conv_sgu_shortconv_step"

def rms_norm(x, g):
    xf = x.astype(jnp.float32)
    y = xf * lax.rsqrt(jnp.mean(xf * xf, axis=-1, keepdims=True) + EPS)
    return (y * g.astype(jnp.float32)).astype(x.dtype)

def layer_norm(x, g, b):
    xf = x.astype(jnp.float32)
    mu = jnp.mean(xf, axis=-1, keepdims=True)
    xc = xf - mu
    var = jnp.mean(xc * xc, axis=-1, keepdims=True)
    y = xc * lax.rsqrt(var + EPS) * g.astype(jnp.float32) + b.astype(jnp.float32)
    return y.astype(x.dtype)

def causal_depthwise_conv(x, buf, w):
    ext = jnp.concatenate([buf.astype(x.dtype), x], axis=1)
    k = w.shape[0]
    y = lax.conv_general_dilated(ext, w.astype(ext.dtype)[:, None, :], window_strides=(1,),
                                 padding="VALID", dimension_numbers=("NWC", "WIO", "NWC"),
                                 feature_group_count=x.shape[-1])
    return y, ext[:, ext.shape[1] - (k - 1):]

def pool_mixer(a, buf, pos0, w_pool, scale):
    bn, t, _ = a.shape
    p = POOL_BUF
    ext = jnp.concatenate([buf.astype(jnp.float32), a.astype(jnp.float32)], axis=1)
    cs = jnp.concatenate([jnp.zeros((bn, 1, GROUP_WIDTH), jnp.float32),
                          jnp.cumsum(ext, axis=1)], axis=1)
    pos = pos0 + jnp.arange(t)
    cur = ext[:, p:]
    outs = []
    for gi, w in enumerate(POOL_WINDOWS):
        sl = slice(gi * SUB_DIM, (gi + 1) * SUB_DIM)
        win_sum = cs[:, p + 1:p + 1 + t, sl] - cs[:, p + 1 - w:p + 1 - w + t, sl]
        cnt = jnp.minimum(w, pos + 1).astype(jnp.float32)[None, :, None]
        outs.append(win_sum / cnt - cur[..., sl])
    d = jnp.stack(outs, axis=2)
    y = jnp.einsum("btgc,gcd->btgd", d, w_pool.astype(jnp.float32)).reshape(bn, t, GROUP_WIDTH)
    y = y * scale.astype(jnp.float32)
    return y.astype(a.dtype), ext[:, ext.shape[1] - p:].astype(a.dtype)

def conformer_conv(z, buf, conv_w, conv_b, ln_g, ln_b):
    p, gate = jnp.split(z, 2, axis=-1)
    g = p * jax.nn.sigmoid(gate)
    c, new_buf = causal_depthwise_conv(g, buf, conv_w)
    c = c + conv_b
    bn, t, _ = c.shape
    c = layer_norm(c.reshape(bn, t, N_SUB, SUB_DIM), ln_g.reshape(N_SUB, SUB_DIM),
                   ln_b.reshape(N_SUB, SUB_DIM))
    return jax.nn.silu(c).reshape(bn, t, GROUP_WIDTH), new_buf

def chunk_spatial_gating(z, ln_g, ln_b, w_s, b_s):
    bn, t, _ = z.shape
    u, v = jnp.split(z, 2, axis=-1)
    v = layer_norm(v.reshape(bn, t, N_SUB, SUB_DIM), ln_g.reshape(N_SUB, SUB_DIM),
                   ln_b.reshape(N_SUB, SUB_DIM))
    n_chunks = -(-t // CHUNK)
    pad = n_chunks * CHUNK - t
    vp = jnp.pad(v, ((0, 0), (0, pad), (0, 0), (0, 0))).reshape(bn, n_chunks, CHUNK, N_SUB, SUB_DIM)
    mask = jnp.tril(jnp.ones((CHUNK, CHUNK), dtype=bool))
    w_causal = jnp.where(mask[None], w_s, jnp.zeros((), w_s.dtype))
    s = jnp.einsum("hts,bnshd->bnthd", w_causal, vp) + jnp.transpose(b_s)[None, None, :, :, None]
    s = s.reshape(bn, n_chunks * CHUNK, N_SUB, SUB_DIM)[:, :t].reshape(bn, t, GROUP_WIDTH)
    return u * s, v.reshape(bn, t, GROUP_WIDTH)

def short_gated_conv(z, buf, w):
    bg, cg, h = jnp.split(z, 3, axis=-1)
    c, new_buf = causal_depthwise_conv(cg * h, buf, w)
    return bg * c, new_buf

def decoder_layer(x, pos0, pool_buf, conv_buf, short_buf, g_mix_pre, g_mix_post, g_ffn_pre,
                  g_ffn_post, w_in, w_out, w_pool, pool_scale, conv_w, conv_b, conv_ln_g,
                  conv_ln_b, sgu_ln_g, sgu_ln_b, sgu_w, sgu_b, short_w, w_up, w_down):
    gw = GROUP_WIDTH
    h = rms_norm(x, g_mix_pre)
    z = h @ w_in
    y_a, nb_pool = pool_mixer(z[..., :gw], pool_buf, pos0, w_pool, pool_scale)
    y_b, nb_conv = conformer_conv(z[..., gw:3 * gw], conv_buf, conv_w, conv_b, conv_ln_g, conv_ln_b)
    y_c, v_rows = chunk_spatial_gating(z[..., 3 * gw:5 * gw], sgu_ln_g, sgu_ln_b, sgu_w, sgu_b)
    y_d, nb_short = short_gated_conv(z[..., 5 * gw:], short_buf, short_w)
    o = jnp.concatenate([y_a, y_b, y_c, y_d], axis=-1) @ w_out
    x = x + rms_norm(o, g_mix_post)
    f = rms_norm(x, g_ffn_pre)
    f = jnp.square(jax.nn.relu(f @ w_up)) @ w_down
    x = x + rms_norm(f, g_ffn_post)
    return x, nb_pool, nb_conv, nb_short, v_rows

def setup_inputs(seed: int = 0) -> dict:
    key = jax.random.key(seed)
    ks = jax.random.split(key, 24)

    def nrm(k, shape, scale):
        return jax.random.normal(k, shape, jnp.float32) * scale

    return {
        "x_prompt": nrm(ks[0], (BATCH, SEQ, D_MODEL), 1.0),
        "x_sample": nrm(ks[1], (DEC_BATCH, DEC_SEQ, D_MODEL), 1.0),
        "state_pool": nrm(ks[2], (DEPTH, DEC_BATCH, POOL_BUF, GROUP_WIDTH), 1.0),
        "state_conv": nrm(ks[3], (DEPTH, DEC_BATCH, CONV_WIDTH - 1, GROUP_WIDTH), 0.5),
        "state_short": nrm(ks[4], (DEPTH, DEC_BATCH, SHORT_WIDTH - 1, GROUP_WIDTH), 1.0),
        "norm_mix_pre": 1.0 + nrm(ks[5], (DEPTH, D_MODEL), 0.1),
        "norm_mix_post": 1.0 + nrm(ks[6], (DEPTH, D_MODEL), 0.1),
        "norm_ffn_pre": 1.0 + nrm(ks[7], (DEPTH, D_MODEL), 0.1),
        "norm_ffn_post": 1.0 + nrm(ks[8], (DEPTH, D_MODEL), 0.1),
        "w_in": nrm(ks[9], (DEPTH, D_MODEL, IN_WIDTH), D_MODEL ** -0.5),
        "w_out": nrm(ks[10], (DEPTH, MIX_WIDTH, D_MODEL), MIX_WIDTH ** -0.5),
        "w_pool": nrm(ks[11], (DEPTH, N_SUB, SUB_DIM, SUB_DIM), SUB_DIM ** -0.5),
        "pool_scale": 1.0 + nrm(ks[12], (DEPTH, GROUP_WIDTH), 0.1),
        "conv_w": nrm(ks[13], (DEPTH, CONV_WIDTH, GROUP_WIDTH), CONV_WIDTH ** -0.5),
        "conv_b": nrm(ks[14], (DEPTH, GROUP_WIDTH), 0.01),
        "conv_ln_g": 1.0 + nrm(ks[15], (DEPTH, GROUP_WIDTH), 0.1),
        "conv_ln_b": nrm(ks[16], (DEPTH, GROUP_WIDTH), 0.01),
        "sgu_ln_g": 1.0 + nrm(ks[17], (DEPTH, GROUP_WIDTH), 0.1),
        "sgu_ln_b": nrm(ks[18], (DEPTH, GROUP_WIDTH), 0.01),
        "sgu_w": nrm(ks[19], (DEPTH, N_SUB, CHUNK, CHUNK), CHUNK ** -0.5),
        "sgu_b": 1.0 + nrm(ks[20], (DEPTH, N_SUB, CHUNK), 0.1),
        "short_w": nrm(ks[21], (DEPTH, SHORT_WIDTH, GROUP_WIDTH), SHORT_WIDTH ** -0.5),
        "w_ffn_up": nrm(ks[22], (DEPTH, D_MODEL, D_FF), D_MODEL ** -0.5),
        "w_ffn_down": nrm(ks[23], (DEPTH, D_FF, D_MODEL), D_FF ** -0.5),
    }

def reference(x_prompt, x_sample, state_pool, state_conv, state_short, norm_mix_pre,
              norm_mix_post, norm_ffn_pre, norm_ffn_post, w_in, w_out, w_pool, pool_scale,
              conv_w, conv_b, conv_ln_g, conv_ln_b, sgu_ln_g, sgu_ln_b, sgu_w, sgu_b, short_w,
              w_ffn_up, w_ffn_down):
    bp = x_prompt.shape[0]
    yp = x_prompt
    ys = x_sample
    pool_p, pool_s, conv_p, conv_s, short_p, short_s, v_s = [], [], [], [], [], [], []
    for l in range(DEPTH):
        params = (norm_mix_pre[l], norm_mix_post[l], norm_ffn_pre[l], norm_ffn_post[l], w_in[l],
                  w_out[l], w_pool[l], pool_scale[l], conv_w[l], conv_b[l], conv_ln_g[l],
                  conv_ln_b[l], sgu_ln_g[l], sgu_ln_b[l], sgu_w[l], sgu_b[l], short_w[l],
                  w_ffn_up[l], w_ffn_down[l])
        yp, pa, pb, pd, _ = decoder_layer(
            yp, 0,
            jnp.zeros((bp, POOL_BUF, GROUP_WIDTH), yp.dtype),
            jnp.zeros((bp, CONV_WIDTH - 1, GROUP_WIDTH), yp.dtype),
            jnp.zeros((bp, SHORT_WIDTH - 1, GROUP_WIDTH), yp.dtype),
            *params)
        ys, sa, sb, sd, sv = decoder_layer(ys, PAST_LEN, state_pool[l], state_conv[l],
                                           state_short[l], *params)
        pool_p.append(pa); pool_s.append(sa)
        conv_p.append(pb); conv_s.append(sb)
        short_p.append(pd); short_s.append(sd)
        v_s.append(sv)
    return (yp, ys, jnp.stack(pool_p), jnp.stack(pool_s), jnp.stack(conv_p), jnp.stack(conv_s),
            jnp.stack(short_p), jnp.stack(short_s), jnp.stack(v_s))


_drawn_inputs = setup_inputs


def setup_inputs(seed=0):
    import zlib

    import numpy as np

    out = dict(_drawn_inputs(seed))
    spreads = {}
    factors = {'conv_b': 8.0, 'conv_ln_b': 8.0, 'sgu_ln_b': 5.711}
    for name, (base, spread) in spreads.items():
        noise = np.random.default_rng([zlib.crc32(name.encode()), seed]).standard_normal(out[name].shape)
        drawn = base * np.exp(spread * noise) if base else spread * noise
        out[name] = __import__('jax').numpy.asarray(drawn.astype(out[name].dtype))
    for name, factor in factors.items():
        out[name] = (out[name] * factor).astype(out[name].dtype)
    return out
```

```python
import concourse.bass as bass
from concourse import mybir
from contextlib import ExitStack


def hybrid_trunk_step(nc, x_prompt, x_sample, state_pool, state_conv, state_short, g_mix_pre, g_mix_post,
                      g_ffn_pre, g_ffn_post, w_in, w_out, w_pool, pool_scale, conv_w, conv_b, conv_ln_g,
                      conv_ln_b, sgu_ln_g, sgu_ln_b, sgu_w, sgu_b, short_w, w_up, w_down,
                      y_prompt, y_sample, new_pool_p, new_pool_s, new_conv_p, new_conv_s,
                      new_short_p, new_short_s, chunk_v_s):
    fp32, f32r = mybir.dt.float32, mybir.dt.float32r
    ALU, ACT, AX = mybir.AluOpType, mybir.ActivationFunctionType, mybir.AxisListType
    PE, DVE, SC, GP = nc.tensor, nc.vector, nc.scalar, nc.gpsimd

    P = 128
    D = x_prompt.shape[2]
    SEQ = x_prompt.shape[1]
    NB_S, NT_S = x_sample.shape[0], x_sample.shape[1]
    NS = NB_S * NT_S
    K = D // P
    GW = D // 4
    PC = 256
    N1 = 512
    B1 = SEQ // N1
    CH = P
    NCH = N1 // CH
    HP, HC, HS = state_pool.shape[2], state_conv.shape[2], state_short.shape[2]
    TAPS, STAPS = HC + 1, HS + 1
    T = SEQ + NS
    B2 = 5
    N2 = T // B2
    Q = w_up.shape[2] // D
    EPS = 1e-6
    HEAD = 64
    TT2 = [(i * P, min(P, N2 - i * P)) for i in range(-(-N2 // P))]

    GATE, PV, AV, CV, HV, VV, UV, BV = range(8)
    COLS = [2 * GW, GW, 0, 6 * GW, 7 * GW, 4 * GW, 3 * GW, 5 * GW]
    NP1 = len(COLS)
    J2 = NP1 * (B1 + 1)
    TD_S = 2 * NP1 * B1
    TD_2 = TD_S + NP1
    TAPS_AT = {1: 4, 2: 7, 3: 7, 4: 5, 5: 4, 6: 4}

    ROWS, at = {}, 0
    for name, arr, n in (("mix_pre", g_mix_pre, K), ("mix_post", g_mix_post, K), ("ffn_pre", g_ffn_pre, K),
                         ("ffn_post", g_ffn_post, K), ("conv_w", conv_w, 2 * TAPS), ("conv_b", conv_b, 2),
                         ("conv_ln_g", conv_ln_g, 2), ("conv_ln_b", conv_ln_b, 2),
                         ("short_w", short_w, 2 * STAPS), ("pool_scale", pool_scale, 2)):
        ROWS[name] = (at, arr, n)
        at += n
    NROW = at

    ctx = ExitStack()
    with ctx:
        def sb(name, shape, dt=fp32, to=ctx):
            return to.enter_context(nc.sbuf_tensor(name, shape, dt))

        def pb(name):
            return ctx.enter_context(nc.psum_tensor(name, [P, 512], fp32))

        def sem(name):
            return ctx.enter_context(nc.semaphore(name))

        xT_d = nc.dram_tensor("xT_scratch", [P, K, T], fp32, kind="Internal").ap()
        mixT_d = nc.dram_tensor("mixT_scratch", [P, K, T], fp32, kind="Internal").ap()

        raw = sb("raw", [P, 2, K, PC])
        w_hi = sb("w_hi", [P, 2, K, PC], f32r)
        w_lo = sb("w_lo", [P, 2, K, PC], f32r)
        ident = sb("ident", [P, P])
        ones = sb("ones", [P, P])
        cst = sb("cst", [P, NROW])
        eps = sb("eps", [P, 1])

        def col(name, i):
            c = ROWS[name][0] + i
            return cst[:, c:c + 1]

        p1 = ExitStack()
        x_tok = sb("x_tok", [P, 2, D], to=p1)
        xT = sb("xT", [P, K, N1], to=p1)
        h_hi = sb("h_hi", [P, K, N1], f32r, to=p1)
        h_lo = sb("h_lo", [P, K, N1], f32r, to=p1)
        h_tmp = sb("h_tmp", [P, 3, N1], to=p1)
        sq1 = sb("sq1", [P, 2, N1], to=p1)
        acc1 = sb("acc1", [P, N1], to=p1)
        root1 = sb("root1", [P, N1], to=p1)
        inv1 = sb("inv1", [P, N1], to=p1)
        sig = sb("sig", [P, 2, N1], to=p1)
        g_ext = sb("g_ext", [P, 2, HC + N1], to=p1)
        a_ext = sb("a_ext", [P, 2, HP + N1], to=p1)
        ch_ext = sb("ch_ext", [P, 2, HS + N1], to=p1)
        win = sb("win", [P, 6, HP + N1], to=p1)
        pool_d = sb("pool_d", [P, 2, N1], to=p1)
        c_gate = sb("c_gate", [P, 2, N1], to=p1)
        c_short = sb("c_short", [P, 2, N1], to=p1)
        conv = sb("conv", [P, 2, N1], to=p1)
        v_raw = sb("v_raw", [P, NCH, PC], to=p1)
        v_n = sb("v_n", [P, NCH, PC], to=p1)
        u_sb = sb("u_sb", [P, 2, N1], to=p1)
        sqcv = sb("sqcv", [P, 2, N1], to=p1)
        inv_c = sb("inv_c", [P, 2, N1], to=p1)
        v_small = sb("v_small", [P, 3, 4 * NCH], to=p1)
        inv_cnt = sb("inv_cnt", [P, 2, HP + 1], to=p1)
        sgu_w_sb = sb("sgu_w_sb", [P, 4, P], to=p1)
        sgu_wT = sb("sgu_wT", [P, 4, P], to=p1)
        sgu_wS = sb("sgu_wS", [NS, 4, NS], to=p1)
        sgu_g = sb("sgu_g", [P, PC], to=p1)
        sgu_bb = sb("sgu_bb", [P, PC], to=p1)
        sgu_bias = sb("sgu_bias", [P, 2, P], to=p1)
        wpool = sb("wpool", [P, 2, P], to=p1)
        headmean = sb("headmean", [P, P], to=p1)
        rows = sb("rows", [NROW, P], to=p1)
        st_pool = sb("st_pool", [NB_S * HP, GW], to=p1)
        st_conv = sb("st_conv", [NB_S // 2 * HC, 2, GW], to=p1)
        st_short = sb("st_short", [NB_S * HS, GW], to=p1)
        as_ext = sb("as_ext", [P, 2, NB_S, HP + NT_S], to=p1)
        gs_ext = sb("gs_ext", [P, 2, NB_S, HC + NT_S], to=p1)
        chs_ext = sb("chs_ext", [P, 2, NB_S, HS + NT_S], to=p1)
        gs_tok = sb("gs_tok", [NS, GW], to=p1)
        chs_tok = sb("chs_tok", [NS, GW], to=p1)
        bs_sb = sb("bs_sb", [P, 2, NS], to=p1)
        st_out = h_tmp[0:HC, :, 0:GW]
        zs = x_tok[0:NS, :, :].rearrange("p a c -> p (a c)")
        p1.close()

        p2 = ExitStack()
        act_hi = sb("act_hi", [P, K, N2], f32r, to=p2)
        act_lo = sb("act_lo", [P, K, N2], f32r, to=p2)
        u_hi = sb("u_hi", [P, 2, K, N2], f32r, to=p2)
        u_lo = sb("u_lo", [P, 2, K, N2], f32r, to=p2)
        o_sb = sb("o_sb", [P, K, N2], to=p2)
        f2_sb = sb("f2_sb", [P, K, N2], to=p2)
        x_in = sb("x_in", [P, K, N2], to=p2)
        x_fin = sb("x_fin", [P, K, N2], to=p2)
        tmp2 = sb("tmp2", [P, 3, N2], to=p2)
        square = sb("square", [P, 2, N2], to=p2)
        relu = sb("relu", [P, 2, N2], to=p2)
        sq2 = sb("sq2", [P, 2, N2], to=p2)
        acc2 = sb("acc2", [P, N2], to=p2)
        root2 = sb("root2", [P, N2], to=p2)
        inv2 = sb("inv2", [P, N2], to=p2)
        y_tok = sb("y_tok", [P, 2, 512], to=p2)
        p2.close()

        mm = [pb(f"mm{i}") for i in range(4)]
        tr = [pb(f"tr{i}") for i in range(2)]
        stat = pb("stat")
        misc = pb("misc")

        s_rows = sem("s_rows")
        s_sguw = sem("s_sguw")
        s_wpool = sem("s_wpool")
        s_bc = sem("s_bc")
        s_wS = sem("s_wS")
        pool_init = sem("pool_init")
        dve_init = sem("dve_init")
        init_tr = sem("init_tr")
        init_copied = sem("init_copied")
        raw_full = [sem(f"raw_full{i}") for i in range(2)]
        hi_ready = sem("hi_ready")
        lo_ready = sem("lo_ready")
        tile_done = sem("tile_done")
        x_full = [sem(f"x_full{i}") for i in range(2)]
        xt_bank = sem("xt_bank")
        xt_copied = sem("xt_copied")
        xt_stored = sem("xt_stored")
        sq_ready = sem("sq_ready")
        sq_summed = sem("sq_summed")
        stat_ready = sem("stat_ready")
        root_ready = sem("root_ready")
        inv_ready = sem("inv_ready")
        h_step = sem("h_step")
        sig_ready = sem("sig_ready")
        g_done = sem("g_done")
        a_ready = sem("a_ready")
        c_ready = sem("c_ready")
        ch_done = sem("ch_done")
        v_ready = sem("v_ready")
        u_ready = sem("u_ready")
        yd_done = sem("yd_done")
        conv_step = sem("conv_step")
        short_step = sem("short_step")
        pool_step = sem("pool_step")
        d_step = sem("d_step")
        cnt_set = sem("cnt_set")
        pool_ready = sem("pool_ready")
        ya_done = sem("ya_done")
        v_step = sem("v_step")
        vsq_ready = sem("vsq_ready")
        vroot_ready = sem("vroot_ready")
        vn_ready = sem("vn_ready")
        sgu_ready = sem("sgu_ready")
        s_done = sem("s_done")
        yc_done = sem("yc_done")
        mean_ready = sem("mean_ready")
        xc_done = sem("xc_done")
        sqc_ready = sem("sqc_ready")
        var_ready = sem("var_ready")
        rootc_ready = sem("rootc_ready")
        cn_step = sem("cn_step")
        sgm_ready = sem("sgm_ready")
        yb_done = sem("yb_done")
        halo = sem("halo")
        mix_st = [sem(f"mix_st{i}") for i in range(4)]
        zs_ready = sem("zs_ready")
        st_tr = sem("st_tr")
        st_copied = sem("st_copied")
        gs_done = sem("gs_done")
        sx_tr = sem("sx_tr")
        sx_copied = sem("sx_copied")
        out_small = sem("out_small")
        act_step = sem("act_step")
        mix_full = sem("mix_full")
        xin_full = sem("xin_full")
        tile_read = sem("tile_read")
        relu_ready = sem("relu_ready")
        u_step = sem("u_step")
        on_ready = sem("on_ready")
        x2_ready = sem("x2_ready")
        f_tmp = sem("f_tmp")
        fn_ready = sem("fn_ready")
        y_ready = sem("y_ready")
        x_moved = sem("x_moved")
        y_tr = sem("y_tr")
        y_evac = sem("y_evac")
        y_st = [sem(f"y_st{i}") for i in range(2)]

        OUT_SMALL = 2 + 3 * NB_S + 1 + 3

        DVE_INIT = 3 + 4 + sum(w - 1 for w in (2, 4, 8, 16))

        block = ctx.enter_context(nc.Block())

        w_in_v = w_in[0].rearrange("(k p) c -> p k c", p=P)
        w_out_v = w_out[0].rearrange("(k p) c -> p k c", p=P)
        w_up_v = w_up[0].rearrange("(k p) c -> p k c", p=P)
        w_dn_v = w_down[0].rearrange("(q k p) c -> q p k c", p=P, k=K)

        PRO = [("O", 0), ("U", 0), ("U", 1)]
        LOOP = [("D", 0), ("U", 2), ("D", 1), ("U", 3), ("D", 2), ("O", 1), ("D", 3), ("U", 4), ("U", 5)]
        EPI = [("D", 0), ("U", 2), ("D", 1), ("U", 3), ("D", 2), ("D", 3)]
        NPRO, NLOOP = 4 * len(PRO), 4 * len(LOOP)

        def half_panels(eng, unrolled):
            if unrolled:
                for i in range(2):
                    yield i
            else:
                with eng.Fori(0, 2) as i:
                    yield i

        def parts(kind, q):
            return [(kind, q)]

        @block.sync
        def _(sp):
            for name, (r0, arr, n) in ROWS.items():
                src = arr.rearrange("o (r c) -> (o r) c", c=P) if len(arr.shape) == 2 else \
                    arr.rearrange("o k (r c) -> (o k r) c", c=P)
                sp.dma_start(rows[r0:r0 + n, :], src).then_inc(s_rows, 16)
            nrows = len(ROWS)
            sp.dma_start(x_tok[:, 0, :], x_prompt[0, 0:P, :]).then_inc(x_full[0], 16)
            sp.dma_start(x_tok[:, 1, :], x_prompt[0, P:2 * P, :]).then_inc(x_full[1], 16)
            for j in range(2):
                sp.dma_start(raw[:, j, :, :], w_in_v[:, :, COLS[j]:COLS[j] + PC]).then_inc(raw_full[j], 16)
            sp.dma_start(st_pool[:, :], state_pool[0].rearrange("b r c -> (b r) c")).then_inc(s_rows, 16)
            for r in range(2):
                sp.dma_start(st_conv[:, r, :], state_conv[0, r * (NB_S // 2):(r + 1) * (NB_S // 2)]
                             .rearrange("b r c -> (b r) c")).then_inc(s_rows, 16)
            sp.dma_start(st_short[:, :], state_short[0].rearrange("b r c -> (b r) c")).then_inc(s_rows, 16)
            for i in range(2, 4):
                sp.wait_ge(xt_bank, 2 * (i - 1))
                sp.dma_start(x_tok[:, i % 2, :], x_prompt[0, i * P:(i + 1) * P, :]).then_inc(x_full[i % 2], 16)
            sp.dma_start(new_pool_s[0, :, 0:HP - NT_S, :], state_pool[0, :, NT_S:HP, :]).then_inc(out_small, 16)
            sp.dma_start(new_conv_s[0, :, 0:HC - NT_S, :], state_conv[0, :, NT_S:HC, :]).then_inc(out_small, 16)
            sp.wait_ge(xt_copied, 8)
            sp.dma_start(xT_d[:, :, 0:N1], xT[:, :, :]).then_inc(xt_stored, 16)

            def load(cond, slot, src):
                sp.wait_ge(lo_ready, cond)
                sp.dma_start(raw[:, slot, :, :], src).then_inc(raw_full[slot], 16)

            def x_rows(at):
                return x_prompt.rearrange("o t d -> (o t d)")[bass.ds(at, P * D)].rearrange("(p d) -> p d", d=D)

            def prompt_block(b, last):
                if not last:
                    x_at = [sp.snap(((b + 1) * N1 + i * P) * D) for i in range(NCH)]
                for jj in range(NP1):
                    n = (jj + 2) % NP1
                    if last and jj >= NP1 - 2:
                        n = jj + 2 - NP1
                    load(NP1 * b + jj + 1, jj % 2, w_in_v[:, :, COLS[n]:COLS[n] + PC])
                    if last:
                        if jj == 0:
                            sp.dma_start(x_tok[0:NS, 0, :], x_sample.rearrange("b t c -> (b t) c"))\
                              .then_inc(x_full[0], 16)
                        continue
                    if jj == 0:
                        for i in range(2):
                            sp.dma_start(x_tok[:, i, :], x_rows(x_at[i]))\
                              .then_inc(x_full[i], 16)
                    if jj in (1, 2):
                        i = jj + 1
                        sp.wait_ge(xt_bank, 8 * (b + 1) + 2 * (i - 1))
                        sp.dma_start(x_tok[:, i % 2, :], x_rows(x_at[i]))\
                          .then_inc(x_full[i % 2], 16)

            with sp.Fori(0, B1 - 1) as b:
                prompt_block(b, False)
            prompt_block(B1 - 1, True)
            for jj in range(NP1):
                src = w_in_v[:, :, COLS[(jj + 2) % NP1]:COLS[(jj + 2) % NP1] + PC] if jj < NP1 - 2 else \
                    w_out_v[:, :, (jj + 2 - NP1) * PC:(jj + 3 - NP1) * PC]
                load(NP1 * B1 + jj + 1, jj % 2, src)

            def source(stage, i, s):
                kind, q = stage
                c = (2 * i + s) * PC
                if kind == "O":
                    return w_out_v[:, :, bass.ds(c, PC)]
                if kind == "U":
                    return w_up_v[:, :, bass.ds((q % Q) * D + c, PC)]
                return w_dn_v[q % Q][:, :, bass.ds(c, PC)]

            def run(stages, p0, nxt, b):
                for n, stage in enumerate(stages):
                    after = stages[n + 1] if n + 1 < len(stages) else nxt
                    pb_ = p0 + 4 * n
                    if stage[0] == "D" and stage[1] == 0 and b is not None:
                        tok = sp.snap((b + 1) * N2)
                        sp.wait_ge(x_moved, b + 1)
                        sp.dma_start(x_in[:, :, :], xT_d[:, :, bass.ds(tok, N2)]).then_inc(xin_full, 16)
                        sp.dma_start(o_sb[:, :, :], mixT_d[:, :, bass.ds(tok, N2)]).then_inc(mix_full, 16)
                    for s in range(2):
                        load(J2 + pb_ + s + 1, s, source(stage, 1, s))
                    if after is not None:
                        for s in range(2):
                            load(J2 + pb_ + 2 + s + 1, s, source(after, 0, s))

            def first_loads():
                sp.wait_ge(xt_stored, 16 * (B1 + 1))
                for m in range(4):
                    sp.wait_ge(mix_st[m], 16 * (B1 + 1))
                sp.wait_ge(out_small, 16 * OUT_SMALL)
                sp.dma_start(o_sb[:, :, :], mixT_d[:, :, 0:N2]).then_inc(mix_full, 16)
                sp.dma_start(x_in[:, :, :], xT_d[:, :, 0:N2]).then_inc(xin_full, 16)

            first_loads()
            run(PRO, 0, LOOP[0], None)
            with sp.Fori(0, B2 - 1) as b:
                run(LOOP, NPRO + NLOOP * b, LOOP[0], b)
            run(EPI, NPRO + NLOOP * (B2 - 1), None, None)
            sp.wait_ge(out_small, 16 * OUT_SMALL)

        @block.gpsimd
        def _(pool):
            GP.memset(ident[:, :], 0.0).then_inc(pool_init, 1)
            GP.memset(ones[:, :], 1.0).then_inc(pool_init, 1)
            GP.memset(eps[:, :], EPS).then_inc(pool_init, 1)
            GP.memset(wpool[:, :, :], 0.0).then_inc(pool_init, 1)
            GP.memset(headmean[:, :], 0.0).then_inc(pool_init, 1)
            GP.memset(sgu_wS[:, :, :], 0.0).then_inc(pool_init, 1)
            pool.wait_ge(pool_init, 6)
            GP.affine_select(out=ident[:, :], in_=ident[:, :], compare_op=ALU.not_equal, fill=1.0,
                             base=0, pattern=[[-1, P]], channel_multiplier=1).then_inc(pool_init, 1)
            for h in range(2):
                pool.wait_ge(pool_init, 7 + h)
                GP.memset(headmean[h * HEAD:(h + 1) * HEAD, h * HEAD:(h + 1) * HEAD], 1.0 / HEAD)\
                  .then_inc(pool_init, 1)
            pool.wait_ge(pool_init, 9)
            pool.dma_start(sgu_w_sb[:, :, :], sgu_w[0].rearrange("h t s -> t h s")).then_inc(s_sguw, 16)
            for g in range(4):
                a, t = (g % 2) * HEAD, g // 2
                pool.dma_start(wpool[a:a + HEAD, t, a:a + HEAD], w_pool[0, g]).then_inc(s_wpool, 16)
                pool.dma_start(sgu_bias[a:a + HEAD, t, :], sgu_b[0, g].partition_broadcast(HEAD)).then_inc(s_bc, 16)
            pool.dma_start(sgu_g[:, :], sgu_ln_g[0].partition_broadcast(P)).then_inc(s_bc, 16)
            pool.dma_start(sgu_bb[:, :], sgu_ln_b[0].partition_broadcast(P)).then_inc(s_bc, 16)
            pool.wait_ge(s_sguw, 16)
            GP.affine_select(out=sgu_w_sb[:, :, :], in_=sgu_w_sb[:, :, :], compare_op=ALU.is_ge, fill=0.0,
                             base=0, pattern=[[0, 4], [-1, P]], channel_multiplier=1).then_inc(pool_init, 1)
            pool.wait_ge(init_copied, 2)
            for b in range(NB_S):
                r = slice(b * NT_S, (b + 1) * NT_S)
                pool.dma_start(sgu_wS[r, :, r], sgu_wT[0:NT_S, :, 0:NT_S]).then_inc(s_wS, 16)

            def sums(S, sq, acc, n):
                pool.wait_ge(sq_summed, (K - 1) * S)
                pool.wait_ge(stat_ready, S)
                for k in range(1, K):
                    pool.wait_ge(sq_ready, K * S + k + 1)
                    if k > 1:
                        pool.wait_ge(sq_summed, (K - 1) * S + k - 1)
                    a = sq[:, 0, 0:n] if k == 1 else acc[:, 0:n]
                    GP.tensor_tensor(acc[:, 0:n], a, sq[:, k % 2, 0:n], ALU.add).then_inc(sq_summed, 1)

            def windows(b, ext, view, n):
                L = HP + n
                pool.wait_ge(d_step, 12 * b)
                up = slice(HEAD, P)
                al = slice(0, P)
                plan = [(al, 0, None, 0, 13, 1), (up, 1, 0, None, 15, 2), (al, 2, None, 1, 1, 1),
                        (al, 3, 2, None, 3, 2), (al, 4, 3, None, 7, 4), (up, 5, 4, None, 15, 8)]
                for i, (pr, out, src, t, lo, sh) in enumerate(plan):
                    pool.wait_ge(pool_step, 6 * b + i)
                    if src is not None:
                        x = view(win[pr, src, :], lo, L)
                        y = view(win[pr, src, :], lo - sh, L - sh)
                    else:
                        x = ext(pr, t, lo, L)
                        y = ext(pr, t, lo - sh, L - sh)
                    GP.tensor_tensor(view(win[pr, out, :], lo, L), x, y, ALU.add).then_inc(pool_step, 1)

            def v_affine(b, n, nc_):
                pool.wait_ge(v_step, 6 * b + 6)
                vv = v_n[0:n, 0:nc_, :]
                GP.tensor_tensor(vv, vv, sgu_g[0:n, :].unsqueeze(1).to_broadcast([n, nc_, PC]), ALU.mult)\
                  .then_inc(vn_ready, 1)
                pool.wait_ge(vn_ready, 2 * b + 1)
                GP.tensor_tensor(vv, vv, sgu_bb[0:n, :].unsqueeze(1).to_broadcast([n, nc_, PC]), ALU.add)\
                  .then_inc(vn_ready, 1)

            def main_view(buf, lo, hi):
                return buf[:, lo:hi]

            def sample_view(buf, lo, hi):
                w = HP + NT_S
                return buf[:, 0:NB_S * w].rearrange("p (b l) -> p b l", b=NB_S)[:, :, lo:hi]

            sums(0, sq1, acc1, N1)
            pool.wait_ge(s_bc, 16 * 6)
            pool.wait_ge(dve_init, DVE_INIT)

            def prompt_block(b, n_next):
                pool.wait_ge(a_ready, 2 * b + 2)
                pool.wait_ge(vn_ready, 2 * b)
                pool.wait_ge(sq_summed, (K - 1) * (b + 1))
                windows(b, lambda pr, t, lo, hi: a_ext[pr, t, lo:hi], main_view, N1)
                pool.wait_ge(pool_step, 6 * (b + 1))
                sums(b + 1, sq1, acc1, n_next)
                v_affine(b, P, NCH)

            with pool.Fori(0, B1 - 1) as b:
                prompt_block(b, N1)
            prompt_block(B1 - 1, NS)
            pool.wait_ge(sx_copied, 10)
            pool.wait_ge(vn_ready, 2 * B1)
            windows(B1, lambda pr, t, lo, hi: as_ext[pr, t, :, lo:hi], sample_view, NT_S)
            pool.wait_ge(pool_step, 6 * (B1 + 1))
            v_affine(B1, NS, 1)

            pool.wait_ge(tile_read, 0)
            S0 = B1 + 1
            for k in range(2):
                sums(S0 + k, sq2, acc2, N2)
            with pool.Fori(0, B2 - 1) as b:
                for k in range(3):
                    sums(S0 + 2 + 3 * b + k, sq2, acc2, N2)
            sums(S0 + 2 + 3 * (B2 - 1), sq2, acc2, N2)

        @block.scalar
        def _(act):
            def split_hi(m, slot, tiles):
                act.wait_ge(raw_full[slot], 16 * (m + 1))
                act.wait_ge(tile_done, tiles)
                SC.activation(w_hi[:, slot, :, :], raw[:, slot, :, :], ACT.Copy).then_inc(hi_ready, 1)

            def squares(S, sq, n, src, ready):
                for k in range(K):
                    ready(k)
                    if k >= 2:
                        act.wait_ge(sq_summed, (K - 1) * S + max(1, k - 2))
                    else:
                        act.wait_ge(sq_summed, (K - 1) * S)
                    SC.activation(sq[:, k % 2, 0:n], src(k), ACT.Square).then_inc(sq_ready, 1)

            def root(S, dst, n):
                act.wait_ge(stat_ready, S + 1)
                act.wait_ge(inv_ready, S)
                SC.activation(dst[:, 0:n], stat[:, 0:n], ACT.Sqrt, bias=eps[:, :], scale=1.0 / D)\
                  .then_inc(root_ready, 1)

            def xt_copy(b, i, n):
                for hh in range(2):
                    act.wait_ge(xt_bank, 8 * b + 2 * i + hh + 1)
                    if i == 0:
                        act.wait_ge(h_step, 24 * b)
                        act.wait_ge(xt_stored, 16 * b)
                    SC.activation(xT[:, 4 * hh:4 * hh + 4, i * P:i * P + n],
                                  tr[hh][:, 0:4 * P].rearrange("p (k t) -> p k t", k=4)[:, :, 0:n],
                                  ACT.Copy).then_inc(xt_copied, 1)

            act.wait_ge(init_tr, 1)
            SC.activation(cst[:, :], tr[0][:, 0:NROW], ACT.Copy).then_inc(init_copied, 1)
            act.wait_ge(init_tr, 2)
            SC.activation(sgu_wT[:, :, :], tr[1][:, :].rearrange("p (h t) -> p h t", h=4), ACT.Copy)\
              .then_inc(init_copied, 1)
            split_hi(0, 0, 0)
            for i in range(NCH):
                xt_copy(0, i, P)
            act.wait_ge(xt_copied, 8)
            squares(0, sq1, N1, lambda k: xT[:, k, :], lambda k: None)
            root(0, root1, N1)

            def prompt_block(b, last):
                n_next = NS if last else N1

                def evac(jj, done, dst):
                    for t in range(2):
                        act.wait_ge(tile_done, 2 * (NP1 * b + jj) + t + 1)
                        SC.activation(dst(t), mm[2 * (jj % 2) + t][:, :], ACT.Copy).then_inc(done, 1)

                for jj in range(NP1):
                    split_hi((NP1 // 2) * b + (jj + 1) // 2, (jj + 1) % 2, 2 * (NP1 * b + jj))
                    if jj == GATE:
                        act.wait_ge(yb_done, 2 * b)
                        for t in range(2):
                            act.wait_ge(tile_done, 2 * (NP1 * b + jj) + t + 1)
                            SC.activation(sig[:, t, :], mm[t][:, :], ACT.Sigmoid).then_inc(sig_ready, 1)
                    if jj == AV:
                        act.wait_ge(halo, 3 * b)
                        act.wait_ge(dve_init, DVE_INIT)
                        evac(jj, a_ready, lambda t: a_ext[:, t, HP:HP + N1])
                    if jj == CV:
                        act.wait_ge(yc_done, 2 * b)
                        evac(jj, c_ready, lambda t: c_gate[:, t, :])
                    if jj == VV:
                        act.wait_ge(v_step, 6 * b)
                        evac(jj, v_ready, lambda t: v_raw[:, 2 * t:2 * t + 2, :].rearrange("p a c -> p (a c)"))
                    if jj == UV:
                        act.wait_ge(mix_st[2], 16 * b)
                        evac(jj, u_ready, lambda t: u_sb[:, t, :])
                    if jj < 4 and (not last or jj == 0):
                        xt_copy(b + 1, jj, NS if last else P)
                    if jj == 3:
                        act.wait_ge(xt_copied, 8 * (b + 1) + (2 if last else 8))
                        act.dma_start(xT_d[:, :, bass.ds((b + 1) * N1, n_next)], xT[:, :, 0:n_next])\
                           .then_inc(xt_stored, 16)
                        squares(b + 1, sq1, n_next, lambda k: xT[:, k, 0:n_next], lambda k: None)
                    if jj == 5:
                        root(b + 1, root1, n_next)
                        act.wait_ge(v_step, 6 * b + 3)
                        act.wait_ge(yb_done, 2 * b)
                        SC.activation(sqcv[:, :, :].rearrange("p a n -> p (a n)"),
                                      v_n[:, :, :].rearrange("p a n -> p (a n)"), ACT.Square).then_inc(vsq_ready, 1)
                    if jj == 6:
                        act.wait_ge(v_step, 6 * b + 4)
                        SC.activation(v_small[:, 2, :], v_small[:, 1, :], ACT.Sqrt, bias=eps[:, :],
                                      scale=1.0 / HEAD).then_inc(vroot_ready, 1)
                    if jj == 7:
                        pool_out(b, N1)
                conv_norm(b, N1)
                store(b * N1, N1, b)

            def pool_out(b, n):
                for t in range(2):
                    act.wait_ge(pool_ready, 2 * b + t + 1)
                    SC.activation(pool_d[:, t, 0:n], tr[t][:, 0:n], ACT.Copy, scale=col("pool_scale", t))\
                      .then_inc(ya_done, 1)

            def conv_norm(b, n):
                for t in range(2):
                    act.wait_ge(xc_done, 2 * b + t + 1)
                    SC.activation(sqcv[:, t, 0:n], conv[:, t, 0:n], ACT.Square).then_inc(sqc_ready, 1)
                for t in range(2):
                    act.wait_ge(var_ready, 2 * b + t + 1)
                    SC.activation(inv_c[:, t, 0:n], tr[t][:, 0:n], ACT.Sqrt, bias=eps[:, :]).then_inc(rootc_ready, 1)
                for t in range(2):
                    act.wait_ge(cn_step, 6 * b + 3 * t + 2)
                    SC.activation(sig[:, t, 0:n], conv[:, t, 0:n], ACT.Sigmoid, bias=col("conv_ln_b", t),
                                  scale=col("conv_ln_g", t)).then_inc(sgm_ready, 1)

            def store(tok, n, b):
                for m, (done, buf) in enumerate(((ya_done, pool_d), (yb_done, conv), (yc_done, u_sb),
                                                 (yd_done, c_short))):
                    act.wait_ge(done, 2 * b + 2)
                    act.dma_start(mixT_d[:, 2 * m:2 * m + 2, bass.ds(tok, n)], buf[:, :, 0:n]).then_inc(mix_st[m], 16)

            with act.Fori(0, B1 - 1) as b:
                prompt_block(b, False)
            prompt_block(B1 - 1, True)

            for t in range(2):
                act.wait_ge(st_tr, t + 1)
                SC.activation(as_ext[:, t, :, 0:HP], tr[t][:, 0:NB_S * HP].rearrange("p (b r) -> p b r", b=NB_S),
                              ACT.Copy).then_inc(st_copied, 1)
            for t in range(2):
                act.wait_ge(st_tr, 2 + t + 1)
                SC.activation(gs_ext[:, t, :, 0:HC], tr[t][:, 0:NB_S * HC].rearrange("p (b r) -> p b r", b=NB_S),
                              ACT.Copy).then_inc(st_copied, 1)
            act.wait_ge(st_tr, 5)
            SC.activation(chs_ext[:, :, :, 0:HS],
                          tr[0][:, 0:2 * NB_S * HS].rearrange("p (a b r) -> p a b r", a=2, b=NB_S),
                          ACT.Copy).then_inc(st_copied, 1)
            act.wait_ge(st_tr, 6)
            SC.activation(st_out[:, 0:2, :], tr[1][0:HC, 0:2 * GW].rearrange("p (a c) -> p a c", a=2), ACT.Copy)\
              .then_inc(st_copied, 1)
            act.wait_ge(st_tr, 7)
            SC.activation(st_out[:, 2, :], tr[0][0:HC, 0:GW], ACT.Copy).then_inc(st_copied, 1)
            act.wait_ge(st_copied, 7)
            act.dma_start(new_pool_p[0, 0], st_out[HC - HP:HC, 0, :]).then_inc(out_small, 16)
            act.dma_start(new_conv_p[0, 0], st_out[0:HC, 1, :]).then_inc(out_small, 16)
            act.dma_start(new_short_p[0, 0], st_out[HC - HS:HC, 2, :]).then_inc(out_small, 16)

            for jj in range(NP1):
                j = NP1 * B1 + jj
                split_hi((j + 1) // 2, (j + 1) % 2, TD_S + jj)
                act.wait_ge(tile_done, TD_S + jj + 1)
                SC.activation(zs[:, COLS[jj]:COLS[jj] + PC], mm[2 * (jj % 2)][0:NS, 0:PC], ACT.Copy)\
                  .then_inc(zs_ready, 1)
                if jj == VV:
                    act.wait_ge(v_step, 6 * B1 + 3)
                    SC.activation(sqcv[0:NS, 0, 0:PC], v_n[0:NS, 0, :], ACT.Square).then_inc(vsq_ready, 1)
                    act.wait_ge(v_step, 6 * B1 + 4)
                    SC.activation(v_small[0:NS, 2, 0:4], v_small[0:NS, 1, 0:4], ACT.Sqrt, bias=eps[0:NS, :],
                                  scale=1.0 / HEAD).then_inc(vroot_ready, 1)
            act.wait_ge(zs_ready, NP1)
            SC.activation(sig[0:NS, 0, 0:PC], zs[:, COLS[GATE]:COLS[GATE] + PC], ACT.Sigmoid).then_inc(sig_ready, 1)
            act.wait_ge(gs_done, 2)
            for b in range(NB_S):
                r = slice(b * NT_S, (b + 1) * NT_S)
                act.dma_start(new_pool_s[0, b, HP - NT_S:HP, :], zs[r, 0:GW]).then_inc(out_small, 16)
                act.dma_start(new_conv_s[0, b, HC - NT_S:HC, :], gs_tok[r, :]).then_inc(out_small, 16)
                act.dma_start(new_short_s[0, b, :, :], chs_tok[b * NT_S + NT_S - HS:(b + 1) * NT_S, :])\
                   .then_inc(out_small, 16)
            for i, dst in enumerate([as_ext[:, 0, :, HP:], as_ext[:, 1, :, HP:], gs_ext[:, 0, :, HC:],
                                     gs_ext[:, 1, :, HC:], chs_ext[:, 0, :, HS:], chs_ext[:, 1, :, HS:],
                                     u_sb[:, 0, 0:NS], u_sb[:, 1, 0:NS], bs_sb[:, 0, :], bs_sb[:, 1, :]]):
                if i == 0:
                    act.wait_ge(sx_tr, 1)
                if i == 6:
                    act.wait_ge(mix_st[2], 16 * B1)
                src = tr[1][:, i * NS:(i + 1) * NS]
                if i < 6:
                    src = src.rearrange("p (b t) -> p b t", b=NB_S)
                SC.activation(dst, src, ACT.Copy).then_inc(sx_copied, 1)
            act.wait_ge(vn_ready, 2 * B1 + 2)
            act.dma_start(chunk_v_s[0].rearrange("b t c -> (b t) c"), v_n[0:NS, 0, :]).then_inc(out_small, 16)
            pool_out(B1, NS)
            conv_norm(B1, NS)
            store(SEQ, NS, B1)

            S0 = B1 + 1

            def step(pan, m, s, last=False):
                if not last:
                    split_hi(J2 // 2 + m + (1 if s else 0), 1 - s, TD_2 + 2 * pan)

            def stage(kind, p0, h0, b, hooks, nloop, S=None, final=False):
                for i in half_panels(act, hooks is not None or kind == "O"):
                    for s in range(2):
                        pan = p0 + 2 * i + s
                        step(pan, h0 + i, s, last=final and i == 1 and s == 1)
                        if kind == "U":
                            for t in range(2):
                                act.wait_ge(tile_done, TD_2 + 2 * pan + t + 1)
                                act.wait_ge(tile_read, 2 * pan + t - 1)
                                SC.activation(relu[:, t, :], mm[2 * s + t][:, 0:N2], ACT.Relu)\
                                  .then_inc(relu_ready, 1)
                        if kind == "O":
                            for t in range(2):
                                k = 4 * i + 2 * s + t
                                act.wait_ge(tile_read, 2 * pan + t + 1)
                                square_one(S, k, o_sb)
                        if hooks is not None:
                            hooks(2 * i + s)

            def square_one(S, k, src):
                act.wait_ge(sq_summed, (K - 1) * S + (max(1, k - 2) if k >= 2 else 0))
                SC.activation(sq2[:, k % 2, :], src[:, k, :], ACT.Square).then_inc(sq_ready, 1)

            def squares_x2(b, S, ks):
                for k in ks:
                    act.wait_ge(x2_ready, K * b + k + 1)
                    square_one(S, k, x_in)

            def y_out(b, i):
                t0, n = TT2[i]
                for hh in range(2):
                    act.wait_ge(y_tr, 8 * b + 2 * i + hh + 1)
                    act.wait_ge(y_st[hh], 16 * (4 * b + i))
                    SC.activation(y_tok[0:n, hh, :], tr[hh][0:n, :], ACT.Copy).then_inc(y_evac, 1)
                for hh in range(2):
                    act.wait_ge(y_evac, 8 * b + 2 * i + hh + 1)
                    cols = slice(hh * 512, (hh + 1) * 512)
                    tok = b * N2 + t0
                    if not isinstance(b, int) or b < B2 - 1 or i < 3:
                        dst = y_prompt[0, bass.ds(tok, n), cols]
                    else:
                        dst = y_sample.rearrange("b t c -> (b t) c")[:, cols]
                    act.dma_start(dst, y_tok[0:n, hh, :]).then_inc(y_st[hh], 16)

            stage("O", 0, 0, 0, None, 0, S=S0)
            root(S0, root2, N2)
            squares_x2(0, S0 + 1, range(K))
            root(S0 + 1, root2, N2)
            stage("U", 4, 2, 0, None, 0)
            stage("U", 8, 4, 0, None, 0)

            def block_stages(b, p, h, S, tail):
                stage("D", p, h, b, None, 0)
                stage("U", p + 4, h + 2, b, None, 0)
                stage("D", p + 8, h + 4, b, None, 0)
                stage("U", p + 12, h + 6, b, None, 0)
                stage("D", p + 16, h + 8, b, None, 0)
                if tail:
                    stage("D", p + 20, h + 10, b, None, 0)
                    return
                stage("O", p + 20, h + 10, b, None, 0, S=S)

                def norms(n):
                    if n == 0:
                        root(S, root2, N2)
                    if n == 1:
                        squares_x2(b + 1, S + 1, range(K))
                    if n == 2:
                        root(S + 1, root2, N2)

                stage("D", p + 24, h + 12, b, norms, 0)

                def finish(n):
                    if n == 0:
                        pass
                    if n == 1:
                        root(S + 2, root2, N2)

                for k in range(K):
                    act.wait_ge(tile_read, 2 * (p + 24) + k + 1)
                    square_one(S + 2, k, f2_sb)
                stage("U", p + 28, h + 14, b, finish, 0)
                stage("U", p + 32, h + 16, b, lambda n: y_out(b, n), 0)

            with act.Fori(0, B2 - 1) as b:
                block_stages(b, NPRO + NLOOP * b, NPRO // 2 + (NLOOP // 2) * b, S0 + 2 + 3 * b, False)
            b = B2 - 1
            p, h, S = NPRO + NLOOP * b, (NPRO + NLOOP * b) // 2, S0 + 2 + 3 * b
            stage("D", p, h, b, None, 0)
            stage("U", p + 4, h + 2, b, None, 0)
            stage("D", p + 8, h + 4, b, None, 0)
            stage("U", p + 12, h + 6, b, None, 0)
            stage("D", p + 16, h + 8, b, None, 0)
            stage("D", p + 20, h + 10, b, lambda n: None, 0, final=True)
            for k in range(K):
                act.wait_ge(tile_read, 2 * (p + 20) + k + 1)
                square_one(S, k, f2_sb)
            root(S, root2, N2)
            for i in range(len(TT2)):
                y_out(b, i)
            for hh in range(2):
                act.wait_ge(y_st[hh], 16 * 4 * B2)

        @block.vector
        def _(dve):
            def split_lo(j, slot):
                dve.wait_ge(hi_ready, j + 1)
                DVE.tensor_tensor(w_lo[:, slot, :, :], raw[:, slot, :, :], w_hi[:, slot, :, :].bitcast(fp32),
                                  ALU.subtract).then_inc(lo_ready, 1)

            def invert(S, src, dst, n, read, val):
                dve.wait_ge(read, val)
                dve.wait_ge(root_ready, S + 1)
                DVE.reciprocal(dst[:, 0:n], src[:, 0:n]).then_inc(inv_ready, 1)

            DVE.memset(g_ext[:, :, 0:HC], 0.0).then_inc(dve_init, 1)
            DVE.memset(a_ext[:, :, 0:HP], 0.0).then_inc(dve_init, 1)
            DVE.memset(ch_ext[:, :, 0:HS], 0.0).then_inc(dve_init, 1)
            WIN = [(0, 0, 2), (HEAD, 0, 4), (0, 1, 8), (HEAD, 1, 16)]
            for a, t, w in WIN:
                DVE.memset(inv_cnt[a:a + HEAD, t, :], 1.0 / w).then_inc(dve_init, 1)
            dve.wait_ge(dve_init, 7)
            n_init = 0
            for a, t, w in WIN:
                for pos in range(w - 1):
                    DVE.memset(inv_cnt[a:a + HEAD, t, pos:pos + 1], 1.0 / (pos + 1)).then_inc(dve_init, 1)
                    n_init += 1
            assert 7 + n_init == DVE_INIT
            dve.wait_ge(dve_init, DVE_INIT)
            split_lo(0, 0)

            def h_parts(b, n, free):
                base = 24 * b

                def scale(k):
                    DVE.scalar_tensor_tensor(out=h_tmp[:, k % 3, 0:n], in0=xT[:, k, 0:n], scalar=col("mix_pre", k),
                                             in1=inv1[:, 0:n], op0=ALU.mult, op1=ALU.mult).then_inc(h_step, 1)

                dve.wait_ge(inv_ready, b + 1)
                scale(0)
                scale(1)
                at = 2
                pos = {0: 1, 1: 2}
                for k in range(K):
                    dve.wait_ge(h_step, base + pos[k])
                    if k == 0:
                        dve.wait_ge(tile_done, free)
                    DVE.tensor_copy(h_hi[:, k, 0:n], h_tmp[:, k % 3, 0:n]).then_inc(h_step, 1)
                    at += 1
                    hi_at = at
                    if k + 2 < K:
                        dve.wait_ge(h_step, base + hi_at - 1)
                        scale(k + 2)
                        at += 1
                        pos[k + 2] = at
                    dve.wait_ge(h_step, base + hi_at)
                    DVE.tensor_tensor(h_lo[:, k, 0:n], h_tmp[:, k % 3, 0:n], h_hi[:, k, 0:n].bitcast(fp32),
                                      ALU.subtract).then_inc(h_step, 1)
                    at += 1

            def tap(b, k, ext, dst):
                for t in range(2):
                    if k == 0:
                        DVE.tensor_scalar(dst(t), ext(t, 0), col("conv_w", 0 + t), col("conv_b", t),
                                          ALU.mult, ALU.add).then_inc(conv_step, 1)
                    else:
                        dve.wait_ge(conv_step, 2 * TAPS * b + 2 * (k - 1) + t + 1)
                        DVE.scalar_tensor_tensor(out=dst(t), in0=ext(t, k), scalar=col("conv_w", 2 * k + t),
                                                 in1=dst(t), op0=ALU.mult, op1=ALU.add).then_inc(conv_step, 1)

            def short(b, ext, dst):
                for k in range(STAPS):
                    for t in range(2):
                        if k == 0:
                            DVE.tensor_scalar(dst(t), ext(t, 0), col("short_w", t), None, ALU.mult)\
                               .then_inc(short_step, 1)
                        else:
                            dve.wait_ge(short_step, 2 * STAPS * b + 2 * (k - 1) + t + 1)
                            DVE.scalar_tensor_tensor(out=dst(t), in0=ext(t, k), scalar=col("short_w", 2 * k + t),
                                                     in1=dst(t), op0=ALU.mult, op1=ALU.add).then_inc(short_step, 1)

            def v_norm(b, n, nc_, src):
                G = 4 * nc_
                vv = v_n[0:n, 0:nc_, :].rearrange("p a (h d) -> p (a h) d", d=HEAD)
                sq = sqcv[0:n, :, :].rearrange("p a n -> p (a n)")[:, 0:G * HEAD].rearrange("p (g d) -> p g d", d=HEAD)
                sm = [v_small[0:n, i, 0:G] for i in range(3)]
                dve.wait_ge(v_step, 6 * b)
                DVE.tensor_reduce(sm[0], src, AX.X, ALU.add).then_inc(v_step, 1)
                dve.wait_ge(v_step, 6 * b + 1)
                DVE.tensor_scalar(sm[1], sm[0], -1.0 / HEAD, None, ALU.mult).then_inc(v_step, 1)
                dve.wait_ge(v_step, 6 * b + 2)
                DVE.tensor_tensor(vv, src, sm[1].unsqueeze(2).to_broadcast([n, G, HEAD]), ALU.add).then_inc(v_step, 1)
                yield
                dve.wait_ge(vsq_ready, b + 1)
                DVE.tensor_reduce(sm[1], sq, AX.X, ALU.add).then_inc(v_step, 1)
                yield
                dve.wait_ge(vroot_ready, b + 1)
                DVE.reciprocal(sm[0], sm[2]).then_inc(v_step, 1)
                dve.wait_ge(v_step, 6 * b + 5)
                DVE.tensor_tensor(vv, vv, sm[0].unsqueeze(2).to_broadcast([n, G, HEAD]), ALU.mult).then_inc(v_step, 1)
                yield

            def pool_diff(b, n, ext, wview, dst, edge):
                dve.wait_ge(pool_step, 6 * b + 6)
                dve.wait_ge(cnt_set, 4 * b)
                dve.wait_ge(mix_st[0], 16 * b)
                cnt = 12 * b
                for (a, t, w), slot in zip(WIN, (0, 1, 4, 5)):
                    pr = slice(a, a + HEAD)
                    e = edge
                    DVE.scalar_tensor_tensor(out=dst(pr, t, e, n), in0=wview(pr, slot, HP + e, HP + n), scalar=1.0 / w,
                                             in1=ext(pr, t, HP + e, HP + n), op0=ALU.mult, op1=ALU.subtract)\
                       .then_inc(d_step, 1)
                    cnt = cnt + 1
                    if e:
                        DVE.tensor_tensor(dst(pr, t, 0, e), wview(pr, slot, HP, HP + e), inv_cnt[pr, t, :], ALU.mult)\
                           .then_inc(d_step, 1)
                        cnt = cnt + 1
                        dve.wait_ge(d_step, cnt)
                        DVE.tensor_tensor(dst(pr, t, 0, e), dst(pr, t, 0, e), ext(pr, t, HP, HP + e), ALU.subtract)\
                           .then_inc(d_step, 1)
                        cnt = cnt + 1

            def centre(b, n):
                for t in range(2):
                    dve.wait_ge(mean_ready, 2 * b + t + 1)
                    DVE.tensor_tensor(conv[:, t, 0:n], conv[:, t, 0:n], tr[t][:, 0:n], ALU.subtract)\
                       .then_inc(xc_done, 1)

            def conv_finish(b, n):
                for t in range(2):
                    dve.wait_ge(rootc_ready, 2 * b + t + 1)
                    DVE.reciprocal(inv_c[:, t, 0:n], inv_c[:, t, 0:n]).then_inc(cn_step, 1)
                    dve.wait_ge(cn_step, 6 * b + 3 * t + 1)
                    DVE.tensor_tensor(conv[:, t, 0:n], conv[:, t, 0:n], inv_c[:, t, 0:n], ALU.mult).then_inc(cn_step, 1)
                    dve.wait_ge(cn_step, 6 * b + 3 * t + 2)
                    DVE.tensor_scalar(sqcv[:, t, 0:n], conv[:, t, 0:n], col("conv_ln_g", t), col("conv_ln_b", t),
                                      ALU.mult, ALU.add).then_inc(cn_step, 1)
                for t in range(2):
                    dve.wait_ge(cn_step, 6 * b + 3 * t + 3)
                    dve.wait_ge(sgm_ready, 2 * b + t + 1)
                    DVE.tensor_tensor(conv[:, t, 0:n], sqcv[:, t, 0:n], sig[:, t, 0:n], ALU.mult).then_inc(yb_done, 1)

            def gate_v(b, n, bias):
                for t, bank in ((0, misc), (1, stat)):
                    dve.wait_ge(sgu_ready, 2 * b + t + 1)
                    if t == 0:
                        dve.wait_ge(ch_done, 2 * b + 2)
                    x, o = bias(bank, t)
                    DVE.tensor_tensor(o, x[0], x[1], ALU.add).then_inc(s_done, 1)
                for t in range(2):
                    dve.wait_ge(s_done, 2 * b + t + 1)
                    DVE.tensor_tensor(u_sb[:, t, 0:n], c_gate[:, t, 0:n], u_sb[:, t, 0:n], ALU.mult)\
                       .then_inc(yc_done, 1)

            def bias_main(bank, t):
                v = "p (c t) -> p c t"
                return ((bank[:, :].rearrange(v, c=NCH), sgu_bias[:, t, :].unsqueeze(1).to_broadcast([P, NCH, CH])),
                        c_gate[:, t, :].rearrange(v, c=NCH))

            def bias_sample(bank, t):
                v = "p (b t) -> p b t"
                return ((bank[:, 0:NS].rearrange(v, b=NB_S),
                         sgu_bias[:, t, 0:NT_S].unsqueeze(1).to_broadcast([P, NB_S, NT_S])),
                        c_gate[:, t, 0:NS].rearrange(v, b=NB_S))

            invert(0, root1, inv1, N1, h_step, 0)
            h_parts(0, N1, 0)

            def prompt_block(b, last):
                n_next = NS if last else N1
                base = NP1 * b
                k0 = 0
                vn = v_norm(b, P, NCH, v_raw[:, :, :].rearrange("p a (h d) -> p (a h) d", d=HEAD))

                def product(jj, ready, other, dst, done):
                    for t in range(2):
                        dve.wait_ge(tile_done, 2 * (base + jj) + t + 1)
                        dve.wait_ge(ready, 2 * b + t + 1)
                        DVE.tensor_tensor(dst(t), mm[2 * (jj % 2) + t][:, :], other(t), ALU.mult).then_inc(done, 1)

                for jj in range(NP1):
                    split_lo(base + jj + 1, (jj + 1) % 2)
                    if jj == PV:
                        dve.wait_ge(mix_st[1], 16 * b)
                        dve.wait_ge(halo, 3 * b)
                        product(jj, sig_ready, lambda t: sig[:, t, :], lambda t: g_ext[:, t, HC:HC + N1], g_done)
                        dve.wait_ge(g_done, 2 * b + 2)
                    if jj == HV:
                        product(jj, c_ready, lambda t: c_gate[:, t, :], lambda t: ch_ext[:, t, HS:HS + N1], ch_done)
                    if jj == 5:
                        pool_diff(b, N1, lambda pr, t, lo, hi: a_ext[pr, t, lo:hi],
                                  lambda pr, s, lo, hi: win[pr, s, lo:hi],
                                  lambda pr, t, lo, hi: pool_d[pr, t, lo:hi], HP + 1)
                        dve.wait_ge(ch_done, 2 * b + 2)
                        dve.wait_ge(mix_st[3], 16 * b)
                        short(b, lambda t, k: ch_ext[:, t, k:k + N1], lambda t: c_short[:, t, :])
                        dve.wait_ge(v_ready, 2 * b + 2)
                        next(vn)
                    if jj == 6:
                        next(vn)
                        invert(b + 1, root1, inv1, n_next, h_step, 24 * (b + 1))
                        next(vn)
                    for _ in range(TAPS_AT.get(jj, 0)):
                        tap(b, k0, lambda t, k: g_ext[:, t, k:k + N1], lambda t: conv[:, t, :])
                        k0 += 1
                    if jj == BV:
                        dve.wait_ge(short_step, 2 * STAPS * (b + 1))
                        product(jj, short_step, lambda t: c_short[:, t, :], lambda t: c_short[:, t, :], yd_done)
                assert k0 == TAPS
                centre(b, N1)
                h_parts(b + 1, n_next, 2 * NP1 * (b + 1))
                gate_v(b, N1, bias_main)
                conv_finish(b, N1)
                dve.wait_ge(d_step, 12 * (b + 1))
                DVE.tensor_copy(g_ext[:, :, 0:HC], g_ext[:, :, N1:N1 + HC]).then_inc(halo, 1)
                DVE.tensor_copy(a_ext[:, :, 0:HP], a_ext[:, :, N1:N1 + HP]).then_inc(halo, 1)
                DVE.tensor_copy(ch_ext[:, :, 0:HS], ch_ext[:, :, N1:N1 + HS]).then_inc(halo, 1)
                for a, t, w in WIN:
                    DVE.memset(inv_cnt[a:a + HEAD, t, :], 1.0 / w).then_inc(cnt_set, 1)

            with dve.Fori(0, B1 - 1) as b:
                prompt_block(b, False)
            prompt_block(B1 - 1, True)

            for jj in range(NP1):
                split_lo(NP1 * B1 + jj + 1, (jj + 1) % 2)
                if jj == VV:
                    dve.wait_ge(zs_ready, jj + 1)
                    vn = v_norm(B1, NS, 1, zs[:, COLS[VV]:COLS[VV] + PC].rearrange("p (h d) -> p h d", d=HEAD))
                    for _ in range(3):
                        next(vn)
            dve.wait_ge(sig_ready, 2 * B1 + 1)
            DVE.tensor_tensor(gs_tok[:, :], zs[:, COLS[PV]:COLS[PV] + PC], sig[0:NS, 0, 0:PC], ALU.mult)\
               .then_inc(gs_done, 1)
            DVE.tensor_tensor(chs_tok[:, :], zs[:, COLS[CV]:COLS[CV] + PC], zs[:, COLS[HV]:COLS[HV] + PC], ALU.mult)\
               .then_inc(gs_done, 1)
            dve.wait_ge(sx_copied, 10)
            s_out = lambda buf, t: buf[:, t, 0:NS].rearrange("p (b t) -> p b t", b=NB_S)
            dve.wait_ge(mix_st[1], 16 * B1)
            for k in range(TAPS):
                tap(B1, k, lambda t, k: gs_ext[:, t, :, k:k + NT_S], lambda t: s_out(conv, t))
            sw = HP + NT_S
            pool_diff(B1, NT_S, lambda pr, t, lo, hi: as_ext[pr, t, :, lo:hi],
                      lambda pr, s, lo, hi: win[pr, s, 0:NB_S * sw].rearrange("p (b l) -> p b l", b=NB_S)[:, :, lo:hi],
                      lambda pr, t, lo, hi: pool_d[pr, t, 0:NS].rearrange("p (b t) -> p b t", b=NB_S), 0)
            dve.wait_ge(mix_st[3], 16 * B1)
            short(B1, lambda t, k: chs_ext[:, t, :, k:k + NT_S], lambda t: s_out(c_short, t))
            dve.wait_ge(short_step, 2 * STAPS * (B1 + 1))
            for t in range(2):
                DVE.tensor_tensor(c_short[:, t, 0:NS], c_short[:, t, 0:NS], bs_sb[:, t, :], ALU.mult).then_inc(yd_done, 1)
            centre(B1, NS)
            for t, bank in ((0, misc), (1, stat)):
                dve.wait_ge(sgu_ready, 2 * B1 + t + 1)
                x, o = bias_sample(bank, t)
                DVE.tensor_tensor(o, x[0], x[1], ALU.add).then_inc(s_done, 1)
            for t in range(2):
                dve.wait_ge(s_done, 2 * B1 + t + 1)
                DVE.tensor_tensor(u_sb[:, t, 0:NS], c_gate[:, t, 0:NS], u_sb[:, t, 0:NS], ALU.mult).then_inc(yc_done, 1)
            conv_finish(B1, NS)

            S0 = B1 + 1

            def act_parts(b, src, ready, base):
                for k in range(K):
                    ready(k)
                    DVE.tensor_copy(act_hi[:, k, :], src(k)).then_inc(act_step, 1)
                    dve.wait_ge(act_step, base + 2 * k + 1)
                    DVE.tensor_tensor(act_lo[:, k, :], src(k), act_hi[:, k, :].bitcast(fp32), ALU.subtract)\
                       .then_inc(act_step, 1)

            def mix_parts(b, tiles):
                dve.wait_ge(mix_full, 16 * (b + 1))
                dve.wait_ge(tile_done, tiles)
                act_parts(b, lambda k: o_sb[:, k, :], lambda k: None, 32 * b)

            def x2_tiles(b, ks):
                for k in ks:
                    DVE.scalar_tensor_tensor(out=o_sb[:, k, :], in0=o_sb[:, k, :], scalar=col("mix_post", k),
                                             in1=inv2[:, :], op0=ALU.mult, op1=ALU.mult).then_inc(on_ready, 1)
                    dve.wait_ge(on_ready, K * b + k + 1)
                    DVE.tensor_tensor(x_in[:, k, :], x_in[:, k, :], o_sb[:, k, :], ALU.add).then_inc(x2_ready, 1)

            def f_tiles(b):
                def scaled(k):
                    if k >= 2:
                        dve.wait_ge(act_step, 32 * b + 16 + 2 * (k - 2))
                    DVE.scalar_tensor_tensor(out=tmp2[:, k % 3, :], in0=x_in[:, k, :], scalar=col("ffn_pre", k),
                                             in1=inv2[:, :], op0=ALU.mult, op1=ALU.mult).then_inc(f_tmp, 1)
                    dve.wait_ge(f_tmp, K * b + k + 1)
                act_parts(b, lambda k: tmp2[:, k % 3, :], scaled, 32 * b + 16)

            def y_tiles(b):
                for k in range(K):
                    DVE.scalar_tensor_tensor(out=f2_sb[:, k, :], in0=f2_sb[:, k, :], scalar=col("ffn_post", k),
                                             in1=inv2[:, :], op0=ALU.mult, op1=ALU.mult).then_inc(fn_ready, 1)
                    dve.wait_ge(fn_ready, K * b + k + 1)
                    DVE.tensor_tensor(f2_sb[:, k, :], f2_sb[:, k, :], x_fin[:, k, :], ALU.add).then_inc(y_ready, 1)

            def inverted(S, read, val):
                invert(S, root2, inv2, N2, read, val)
                dve.wait_ge(inv_ready, S + 1)

            def move_x():
                DVE.tensor_copy(x_fin[:, :, :], x_in[:, :, :]).then_inc(x_moved, 1)

            def stage(kind, p0, up0=0, hooks=None, q=0, final=False, b=0):
                for i in half_panels(dve, hooks is not None):
                    for s in range(2):
                        pan = p0 + 2 * i + s
                        if not (final and i == 1 and s == 1):
                            split_lo(J2 + pan + 1, 1 - s)
                        for t in range(2):
                            bank = mm[2 * s + t][:, 0:N2]
                            k = 4 * i + 2 * s + t
                            if kind == "U":
                                dve.wait_ge(relu_ready, up0 + k + 1)
                                dve.wait_ge(u_step, 2 * (up0 + k))
                                DVE.scalar_tensor_tensor(out=square[:, t, :], in0=bank, scalar=0.0, in1=relu[:, t, :],
                                                         op0=ALU.max, op1=ALU.mult).then_inc(tile_read, 1)
                                dve.wait_ge(tile_read, 2 * pan + t + 1)
                                DVE.tensor_copy(u_hi[:, q % 2, k, :], square[:, t, :]).then_inc(u_step, 1)
                                dve.wait_ge(u_step, 2 * (up0 + k) + 1)
                                DVE.tensor_tensor(u_lo[:, q % 2, k, :], square[:, t, :],
                                                  u_hi[:, q % 2, k, :].bitcast(fp32), ALU.subtract).then_inc(u_step, 1)
                            else:
                                dve.wait_ge(tile_done, TD_2 + 2 * pan + t + 1)
                                if kind == "O":
                                    dve.wait_ge(act_step, 32 * b + 16)
                                    DVE.tensor_copy(o_sb[:, k, :], bank).then_inc(tile_read, 1)
                                elif q == 0:
                                    dve.wait_ge(y_tr, 8 * b)
                                    DVE.tensor_copy(f2_sb[:, k, :], bank).then_inc(tile_read, 1)
                                else:
                                    DVE.tensor_tensor(f2_sb[:, k, :], bank, f2_sb[:, k, :], ALU.add)\
                                       .then_inc(tile_read, 1)
                        if hooks is not None:
                            hooks(2 * i + s)

            mix_parts(0, TD_2)
            stage("O", 0)
            inverted(S0, y_ready, 0)
            dve.wait_ge(xin_full, 16)
            x2_tiles(0, range(K))
            inverted(S0 + 1, on_ready, K)
            f_tiles(0)
            move_x()
            stage("U", 4, 0, q=0)
            stage("U", 8, K, q=1)

            def first_half(b, p):
                up = 4 * K * b
                stage("D", p, q=0, b=b)
                stage("U", p + 4, up + 2 * K, q=2)
                stage("D", p + 8, q=1)
                stage("U", p + 12, up + 3 * K, q=3)

            with dve.Fori(0, B2 - 1) as b:
                p, S = NPRO + NLOOP * b, S0 + 2 + 3 * b
                first_half(b, p)

                def mix_hook(n):
                    if n == 0:
                        mix_parts(b + 1, TD_2 + 2 * (p + 16))

                def norms(n):
                    if n == 0:
                        inverted(S, y_ready, K * b)
                        dve.wait_ge(xin_full, 16 * (b + 2))
                        x2_tiles(b + 1, range(0, 4))
                    if n == 1:
                        x2_tiles(b + 1, range(4, K))
                    if n == 2:
                        inverted(S + 1, on_ready, K * (b + 2))
                        f_tiles(b + 1)

                def finish(n):
                    if n == 1:
                        inverted(S + 2, act_step, 32 * (b + 2))
                        y_tiles(b)
                        dve.wait_ge(y_ready, K * (b + 1))
                        move_x()

                stage("D", p + 16, q=2, hooks=mix_hook)
                stage("O", p + 20, b=b + 1)
                stage("D", p + 24, q=3, hooks=norms)
                stage("U", p + 28, 4 * K * (b + 1), hooks=finish, q=4)
                stage("U", p + 32, 4 * K * (b + 1) + K, q=5)
            b = B2 - 1
            p, S = NPRO + NLOOP * b, S0 + 2 + 3 * b
            first_half(b, p)
            stage("D", p + 16, q=2)
            stage("D", p + 20, q=3, hooks=lambda n: None, final=True)
            inverted(S, y_ready, K * b)
            y_tiles(b)

        @block.tensor
        def _(pe):
            def three(out, whi, wlo, xhi, xlo, k):
                PE.matmul(out, whi, xhi, start=(k == 0), stop=False)
                PE.matmul(out, whi, xlo, start=False, stop=False)
                return PE.matmul(out, wlo, xhi, start=False, stop=(k == K - 1))

            def head_stat(bank, src, n, done):
                PE.matmul(bank[:, 0:n], headmean[:, :], src[:, 0:n], start=True, stop=True).then_inc(done, 1)

            pe.wait_ge(pool_init, 9)
            pe.wait_ge(s_rows, 16 * (len(ROWS) + 4))
            PE.transpose(tr[0][:, 0:NROW], rows[:, :], ident[0:NROW, 0:NROW]).then_inc(init_tr, 1)
            pe.wait_ge(pool_init, 10)
            for h in range(4):
                last = PE.transpose(tr[1][:, h * P:(h + 1) * P], sgu_w_sb[:, h, :], ident[:, :])
            last.then_inc(init_tr, 1)

            def transpose_x(b, i, n):
                s = i % 2
                pe.wait_ge(x_full[s], 16 * (2 * b + i // 2 + 1))
                for hh in range(2):
                    if i > 0:
                        pe.wait_ge(xt_copied, 8 * b + 2 * (i - 1) + hh + 1)
                    for kk in range(4):
                        k = 4 * hh + kk
                        last = PE.transpose(tr[hh][:, kk * P:kk * P + n], x_tok[0:n, s, k * P:(k + 1) * P],
                                            ident[0:n, 0:n])
                    last.then_inc(xt_bank, 1)

            def norm_sum(S, acc, n):
                pe.wait_ge(sq_summed, (K - 1) * (S + 1))
                pe.wait_ge(root_ready, S)
                PE.matmul(stat[:, 0:n], ones[:, :], acc[:, 0:n], start=True, stop=True).then_inc(stat_ready, 1)

            pe.wait_ge(init_copied, 2)
            for i in range(NCH):
                transpose_x(0, i, P)
            norm_sum(0, acc1, N1)

            def h_wait(b, k):
                pe.wait_ge(h_step, 24 * b + (24 if k == K - 1 else 5 + 3 * k if k < K - 2 else 22))

            def prompt_block(b, last):
                base = NP1 * b
                frees = {0: u_ready, 1: yd_done, 2: sig_ready, 3: g_done, 4: a_ready, 5: c_ready, 6: ch_done,
                         7: v_ready}
                for jj in range(NP1):
                    s = jj % 2
                    pe.wait_ge(lo_ready, base + jj + 1)
                    for t in range(2):
                        bank = mm[2 * s + t]
                        pe.wait_ge(frees[jj], 2 * b if jj < 2 else 2 * b + t + 1)
                        if jj != VV:
                            for k in range(K):
                                if jj == 0 and t == 0:
                                    h_wait(b, k)
                                c = slice(t * P, (t + 1) * P)
                                last_mm = three(bank[:, :], w_hi[:, s, k, c], w_lo[:, s, k, c], h_hi[:, k, :],
                                                h_lo[:, k, :], k)
                        else:
                            for half in range(2):
                                r = slice((2 * t + half) * P, (2 * t + half + 1) * P)
                                for k in range(K):
                                    last_mm = three(bank[:, half * PC:(half + 1) * PC], h_hi[:, k, r], h_lo[:, k, r],
                                                    w_hi[:, s, k, :], w_lo[:, s, k, :], k)
                        last_mm.then_inc(tile_done, 1)
                    if jj == 0:
                        pe.wait_ge(rootc_ready, 2 * b)
                    if jj < 4 and (not last or jj == 0):
                        transpose_x(b + 1, jj, NS if last else P)
                    if jj == 4:
                        pe.wait_ge(s_done, 2 * b)
                        norm_sum(b + 1, acc1, NS if last else N1)
                    if jj == 6:
                        pooled(b, N1, xt_copied, 8 * (b + 1) + (2 if last else 8))
                gating(b, N1, b + 2)
                for t in range(2):
                    pe.wait_ge(conv_step, 2 * TAPS * b + 2 * (TAPS - 1) + t + 1)
                    pe.wait_ge(ya_done, 2 * b + t + 1)
                    head_stat(tr[t], conv[:, t, :], N1, mean_ready)
                for t in range(2):
                    pe.wait_ge(sqc_ready, 2 * b + t + 1)
                    head_stat(tr[t], sqcv[:, t, :], N1, var_ready)

            def pooled(b, n, free, val):
                pe.wait_ge(free, val)
                pe.wait_ge(s_wpool, 16 * 4)
                pe.wait_ge(d_step, 12 * b + (12 if n == N1 else 4))
                for t in range(2):
                    PE.matmul(tr[t][:, 0:n], wpool[:, t, :], pool_d[:, t, 0:n], start=True, stop=True)\
                      .then_inc(pool_ready, 1)

            def gating(b, n, S):
                pe.wait_ge(vn_ready, 2 * b + 2)
                pe.wait_ge(s_done, 2 * b)
                pe.wait_ge(root_ready, S)
                for t, bank in ((0, misc), (1, stat)):
                    for h in range(2):
                        c = slice((2 * t + h) * HEAD, (2 * t + h + 1) * HEAD)
                        o = slice(h * HEAD, (h + 1) * HEAD)
                        if n == N1:
                            for ci in range(NCH):
                                last = PE.matmul(bank[o, ci * CH:(ci + 1) * CH], v_n[:, ci, c],
                                                 sgu_wT[:, 2 * t + h, :], start=True, stop=True)
                        else:
                            last = PE.matmul(bank[o, 0:NS], v_n[0:NS, 0, c], sgu_wS[:, 2 * t + h, :],
                                             start=True, stop=True)
                    last.then_inc(sgu_ready, 1)

            with pe.Fori(0, B1 - 1) as b:
                prompt_block(b, False)
            prompt_block(B1 - 1, True)

            pe.wait_ge(rootc_ready, 2 * B1)
            for t in range(2):
                n = NB_S * HP
                PE.transpose(tr[t][:, 0:n], st_pool[:, t * P:(t + 1) * P], ident[0:n, 0:n]).then_inc(st_tr, 1)
            for t in range(2):
                n = NB_S // 2 * HC
                pe.wait_ge(st_copied, t + 1)
                for r in range(2):
                    last = PE.transpose(tr[t][:, r * n:(r + 1) * n], st_conv[:, r, t * P:(t + 1) * P], ident[0:n, 0:n])
                last.then_inc(st_tr, 1)
            pe.wait_ge(st_copied, 3)
            n = NB_S * HS
            for t in range(2):
                last = PE.transpose(tr[0][:, t * n:(t + 1) * n], st_short[:, t * P:(t + 1) * P], ident[0:n, 0:n])
            last.then_inc(st_tr, 1)
            pe.wait_ge(st_copied, 4)
            pe.wait_ge(halo, 3 * B1)
            for i, (ext, hist) in enumerate(((a_ext, HP), (g_ext, HC))):
                for t in range(2):
                    last = PE.transpose(tr[1][0:HC, i * GW + t * P:i * GW + (t + 1) * P],
                                        ext[:, t, N1 + hist - HC:N1 + hist], ident[:, :])
            last.then_inc(st_tr, 1)
            pe.wait_ge(st_copied, 5)
            for t in range(2):
                last = PE.transpose(tr[0][0:HC, t * P:(t + 1) * P], ch_ext[:, t, N1 + HS - HC:N1 + HS], ident[:, :])
            last.then_inc(st_tr, 1)

            for jj in range(NP1):
                s = jj % 2
                pe.wait_ge(lo_ready, NP1 * B1 + jj + 1)
                if jj < 2:
                    pe.wait_ge(u_ready if jj == 0 else yd_done, 2 * B1)
                else:
                    pe.wait_ge(zs_ready, jj - 1)
                for k in range(K):
                    if jj == 0:
                        h_wait(B1, k)
                    last_mm = three(mm[2 * s][0:NS, 0:PC], h_hi[:, k, 0:NS], h_lo[:, k, 0:NS],
                                    w_hi[:, s, k, :], w_lo[:, s, k, :], k)
                last_mm.then_inc(tile_done, 1)
            pe.wait_ge(gs_done, 2)
            pe.wait_ge(st_copied, 7)
            srcs = [zs[:, COLS[AV] + t * P:COLS[AV] + (t + 1) * P] for t in range(2)]
            srcs += [gs_tok[:, t * P:(t + 1) * P] for t in range(2)]
            srcs += [chs_tok[:, t * P:(t + 1) * P] for t in range(2)]
            srcs += [zs[:, COLS[UV] + t * P:COLS[UV] + (t + 1) * P] for t in range(2)]
            srcs += [zs[:, COLS[BV] + t * P:COLS[BV] + (t + 1) * P] for t in range(2)]
            for i, src in enumerate(srcs):
                last = PE.transpose(tr[1][:, i * NS:(i + 1) * NS], src, ident[0:NS, 0:NS])
            last.then_inc(sx_tr, 1)
            pe.wait_ge(s_wS, 16 * NB_S)
            pooled(B1, NS, sx_copied, 10)
            gating(B1, NS, B1 + 1)
            for t in range(2):
                pe.wait_ge(conv_step, 2 * TAPS * (B1 + 1))
                pe.wait_ge(ya_done, 2 * B1 + t + 1)
                head_stat(tr[t], conv[:, t, :], NS, mean_ready)
            for t in range(2):
                pe.wait_ge(sqc_ready, 2 * B1 + t + 1)
                head_stat(tr[t], sqcv[:, t, :], NS, var_ready)

            S0 = B1 + 1

            def stage(kind, p0, b=0, u_need=0, q=0, hooks=None, first=False):
                for i in half_panels(pe, hooks is not None or first):
                    for s in range(2):
                        pan = p0 + 2 * i + s
                        pe.wait_ge(lo_ready, J2 + pan + 1)
                        if kind == "O" and s == 0:
                            pe.wait_ge(act_step, 32 * b + 16)
                        if kind == "D" and s == 0:
                            pe.wait_ge(u_step, u_need)
                        for t in range(2):
                            if first and i == 0:
                                pe.wait_ge(zs_ready, NP1)
                            else:
                                pe.wait_ge(tile_read, 2 * pan + t - 3)
                            for k in range(K):
                                if kind == "U" and s == 0 and t == 0:
                                    pe.wait_ge(act_step, 32 * b + 16 + 2 * (k + 1))
                                c = slice(t * P, (t + 1) * P)
                                hi = u_hi[:, q % 2, k, :] if kind == "D" else act_hi[:, k, :]
                                lo = u_lo[:, q % 2, k, :] if kind == "D" else act_lo[:, k, :]
                                last_mm = three(mm[2 * s + t][:, 0:N2], w_hi[:, s, k, c], w_lo[:, s, k, c], hi, lo, k)
                            last_mm.then_inc(tile_done, 1)
                        if hooks is not None:
                            hooks(2 * i + s)

            def transpose_y(b, i):
                t0, n = TT2[i]
                pe.wait_ge(y_ready, K * (b + 1))
                for hh in range(2):
                    pe.wait_ge(y_evac, 8 * b + (2 * (i - 1) + hh + 1 if i > 0 else 0))
                    for kk in range(4):
                        last = PE.transpose(tr[hh][0:n, kk * P:(kk + 1) * P], f2_sb[:, 4 * hh + kk, t0:t0 + n],
                                            ident[:, :])
                    last.then_inc(y_tr, 1)

            stage("O", 0, 0, first=True)
            norm_sum(S0, acc2, N2)
            norm_sum(S0 + 1, acc2, N2)
            stage("U", 4, 0)
            stage("U", 8, 0)

            def first_half(b, p):
                u0 = 2 * K * 4 * b
                stage("D", p, b, u0 + 2 * K, 0)
                stage("U", p + 4, b)
                stage("D", p + 8, b, u0 + 4 * K, 1)
                stage("U", p + 12, b)
                stage("D", p + 16, b, u0 + 6 * K, 2)

            with pe.Fori(0, B2 - 1) as b:
                p, S = NPRO + NLOOP * b, S0 + 2 + 3 * b
                first_half(b, p)
                stage("O", p + 20, b + 1)

                def norms(n):
                    if n == 0:
                        norm_sum(S, acc2, N2)
                    if n == 2:
                        norm_sum(S + 1, acc2, N2)

                def finish(n):
                    if n == 0:
                        norm_sum(S + 2, acc2, N2)

                stage("D", p + 24, b, 2 * K * 4 * (b + 1), 3, hooks=norms)
                stage("U", p + 28, b + 1, hooks=finish)
                stage("U", p + 32, b + 1, hooks=lambda n: transpose_y(b, n))
            b = B2 - 1
            p, S = NPRO + NLOOP * b, S0 + 2 + 3 * b
            first_half(b, p)
            stage("D", p + 20, b, 2 * K * 4 * (b + 1), 3)
            norm_sum(S, acc2, N2)
            for i in range(len(TT2)):
                transpose_y(b, i)


_INS = ["x_prompt", "x_sample", "state_pool", "state_conv", "state_short", "norm_mix_pre", "norm_mix_post",
        "norm_ffn_pre", "norm_ffn_post", "w_in", "w_out", "w_pool", "pool_scale", "conv_w", "conv_b",
        "conv_ln_g", "conv_ln_b", "sgu_ln_g", "sgu_ln_b", "sgu_w", "sgu_b", "short_w", "w_ffn_up", "w_ffn_down"]


def kernel(**inputs):
    import numpy as np
    import concourse.bacc as bacc
    from concourse import mybir as mb
    from concourse.bass_utils import run_bass_kernel_spmd as run

    nc = bacc.Bacc("TRN2", target_bir_lowering=False, num_devices=1)
    arrays, args = {}, []
    for name in _INS:
        a = np.ascontiguousarray(inputs[name])
        arrays[f"in_{name}"] = a
        args.append(nc.dram_tensor(f"in_{name}", a.shape, mb.dt.from_np(a.dtype), kind="ExternalInput").ap())
    ins = {n: arrays[f"in_{n}"] for n in _INS}
    outs = [ins["x_prompt"].shape, ins["x_sample"].shape]
    for st in ("state_pool", "state_conv", "state_short"):
        d, b, r, c = ins[st].shape
        outs += [(d, ins["x_prompt"].shape[0], r, c), (d, b, r, c)]
    outs.append((ins["state_pool"].shape[0],) + ins["x_sample"].shape[:2] + (ins["state_pool"].shape[3],))
    for i, shape in enumerate(outs):
        args.append(nc.dram_tensor(f"out_{i}", shape, mb.dt.float32, kind="ExternalOutput").ap())
    hybrid_trunk_step(nc, *args)
    r = run(nc, [arrays], core_ids=[0])
    return tuple(r.results[0][f"out_{i}"] for i in range(len(outs)))
```
